# Optimizing a Trainium2 kernel written in Bass

```python
import math
import jax, jax.numpy as jnp
from jax import lax
import numpy as np

D_MODEL = 1024
BATCH = 1
SEQ = 512
DEPTH = 2
DEC_BATCH = 8
DEC_SEQ = 8
PAST_LEN = 2048
PAGE_SIZE = 128

N_MIXERS = 2
N_ATTN_LAYERS = (DEPTH + 1) // 2
N_GLA_LAYERS = DEPTH // 2
EPS = 1e-6
WINDOW = 128
HEAD_DIM = 64
N_HEADS = D_MODEL // HEAD_DIM
N_KV_HEADS = 4
GROUP = N_HEADS // N_KV_HEADS
Q_DIM = N_HEADS * HEAD_DIM
KV_DIM = N_KV_HEADS * HEAD_DIM
GLA_HEADS = 4
GLA_DK = D_MODEL // 2
GLA_DV = D_MODEL
GLA_DK_HEAD = GLA_DK // GLA_HEADS
GLA_DV_HEAD = GLA_DV // GLA_HEADS
GLA_GATE_RANK = 16
GLA_GATE_NORMALIZER = 16.0
GLA_CHUNK = 64
GLA_IN_DIM = 2 * GLA_DK + 2 * GLA_DV + GLA_GATE_RANK
D_FF = -(-(8 * D_MODEL) // (3 * 256)) * 256

kernel_name = 'swa_gla_hybrid_decode_step'

def rmsnorm(x, g):
    xf = x.astype(jnp.float32)
    r = lax.rsqrt(jnp.mean(xf * xf, axis=-1, keepdims=True) + EPS)
    return (xf * r * g.astype(jnp.float32)).astype(x.dtype)

def alibi_slopes(n):
    return jnp.exp2(-8.0 * jnp.arange(1, n + 1, dtype=jnp.float32) / n)

def swa_attend(q, k, v, q_pos, k_pos, sinks):
    s = jnp.einsum('bnqkgd,bnskd->bnkgqs', q, k, preferred_element_type=jnp.float32) * (HEAD_DIM ** -0.5)
    dist = q_pos[:, :, None] - k_pos[:, None, :]
    valid = (dist >= 0) & (dist <= WINDOW) & (k_pos[:, None, :] >= 0)
    slopes = alibi_slopes(N_HEADS).reshape(N_KV_HEADS, GROUP)
    s = s - slopes[None, None, :, :, None, None] * dist.astype(jnp.float32)[None, :, None, None, :, :]
    s = jnp.where(valid[None, :, None, None, :, :], s, -jnp.inf)
    sink = sinks.astype(jnp.float32).reshape(N_KV_HEADS, GROUP)[None, None, :, :, None, None]
    m = jnp.maximum(jnp.max(s, axis=-1, keepdims=True), sink)
    p = jnp.exp(s - m)
    denom = jnp.sum(p, axis=-1, keepdims=True) + jnp.exp(sink - m)
    return jnp.einsum('bnkgqs,bnskd->bnqkgd', (p / denom).astype(v.dtype), v)

def swa_project(h, w_in):
    proj = h @ w_in
    return jnp.split(proj, [Q_DIM, Q_DIM + KV_DIM], axis=-1)

def swa_prompt(h, w_in, w_out, sinks):
    B, L, _ = h.shape
    q, k, v = swa_project(h, w_in)
    nb = L // WINDOW
    q = q.reshape(B, nb, WINDOW, N_KV_HEADS, GROUP, HEAD_DIM)
    k = k.reshape(B, L, N_KV_HEADS, HEAD_DIM)
    v = v.reshape(B, L, N_KV_HEADS, HEAD_DIM)
    pad = jnp.zeros((B, WINDOW, N_KV_HEADS, HEAD_DIM), k.dtype)
    kp = jnp.concatenate([pad, k], axis=1).reshape(B, nb + 1, WINDOW, N_KV_HEADS, HEAD_DIM)
    vp = jnp.concatenate([pad, v], axis=1).reshape(B, nb + 1, WINDOW, N_KV_HEADS, HEAD_DIM)
    k_ctx = jnp.concatenate([kp[:, :-1], kp[:, 1:]], axis=2)
    v_ctx = jnp.concatenate([vp[:, :-1], vp[:, 1:]], axis=2)
    blk = jnp.arange(nb, dtype=jnp.int32)[:, None] * WINDOW
    q_pos = blk + jnp.arange(WINDOW, dtype=jnp.int32)[None]
    k_pos = blk - WINDOW + jnp.arange(2 * WINDOW, dtype=jnp.int32)[None]
    o = swa_attend(q, k_ctx, v_ctx, q_pos, k_pos, sinks).reshape(B, L, Q_DIM)
    return o @ w_out, k[:, L - WINDOW:], v[:, L - WINDOW:]

def swa_sample(h, k_buf, v_buf, w_in, w_out, sinks):
    B, L, _ = h.shape
    q, k, v = swa_project(h, w_in)
    q = q.reshape(B, 1, L, N_KV_HEADS, GROUP, HEAD_DIM)
    k_ctx = jnp.concatenate([k_buf.astype(k.dtype), k.reshape(B, L, N_KV_HEADS, HEAD_DIM)], axis=1)
    v_ctx = jnp.concatenate([v_buf.astype(v.dtype), v.reshape(B, L, N_KV_HEADS, HEAD_DIM)], axis=1)
    q_pos = (PAST_LEN + jnp.arange(L, dtype=jnp.int32))[None]
    k_pos = (PAST_LEN - WINDOW + jnp.arange(WINDOW + L, dtype=jnp.int32))[None]
    o = swa_attend(q, k_ctx[:, None], v_ctx[:, None], q_pos, k_pos, sinks).reshape(B, L, Q_DIM)
    return o @ w_out, k_ctx[:, L:], v_ctx[:, L:]

def gla_core(q, k, v, log_a, s0):
    B, L, H, DK = q.shape
    DV = v.shape[-1]
    c = math.gcd(L, GLA_CHUNK)
    n = L // c
    q = (q.astype(jnp.float32) * (DK ** -0.5)).reshape(B, n, c, H, DK)
    k = k.astype(jnp.float32).reshape(B, n, c, H, DK)
    v = v.astype(jnp.float32).reshape(B, n, c, H, DV)
    b = jnp.cumsum(log_a.astype(jnp.float32).reshape(B, n, c, H, DK), axis=2)
    b_ref = b[:, :, c // 2:c // 2 + 1]
    b_end = b[:, :, -1:]
    a_mat = jnp.einsum('bnthd,bnshd->bnhts', q * jnp.exp(b - b_ref), k * jnp.exp(b_ref - b))
    causal = jnp.tril(jnp.ones((c, c), dtype=bool))
    a_mat = jnp.where(causal, a_mat, 0.0)
    o_intra = jnp.einsum('bnhts,bnshv->bnthv', a_mat, v)
    q_in = jnp.moveaxis(q * jnp.exp(b), 1, 0)
    k_end = jnp.moveaxis(k * jnp.exp(b_end - b), 1, 0)
    v_s = jnp.moveaxis(v, 1, 0)
    dec = jnp.moveaxis(jnp.exp(b_end[:, :, 0]), 1, 0)

    def step(S, inp):
        qc, kc, vc, dc = inp
        o = jnp.einsum('bthd,bhdv->bthv', qc, S)
        S = dc[..., None] * S + jnp.einsum('bshd,bshv->bhdv', kc, vc)
        return S, o

    s_fin, o_inter = lax.scan(step, s0.astype(jnp.float32), (q_in, k_end, v_s, dec))
    o = o_intra + jnp.moveaxis(o_inter, 0, 1)
    return o.reshape(B, L, H, DV), s_fin

def gla_mixer(h, s0, w_in, w_gate_up, b_gate, norm_g, w_out):
    B, L, _ = h.shape
    q, k, v, r, gd = jnp.split(h @ w_in, [GLA_DK, 2 * GLA_DK, 2 * GLA_DK + GLA_DV, 2 * GLA_DK + 2 * GLA_DV], axis=-1)
    log_a = jax.nn.log_sigmoid((gd @ w_gate_up + b_gate).astype(jnp.float32)) / GLA_GATE_NORMALIZER
    o, s_fin = gla_core(q.reshape(B, L, GLA_HEADS, GLA_DK_HEAD),
                        k.reshape(B, L, GLA_HEADS, GLA_DK_HEAD),
                        v.reshape(B, L, GLA_HEADS, GLA_DV_HEAD),
                        log_a.reshape(B, L, GLA_HEADS, GLA_DK_HEAD), s0)
    o = rmsnorm(o, norm_g).reshape(B, L, GLA_DV) * jax.nn.silu(r.astype(jnp.float32))
    return o.astype(h.dtype) @ w_out, s_fin

def swiglu_ffn(h, w_in, w_out):
    g, u = jnp.split(h @ w_in, [D_FF], axis=-1)
    return (jax.nn.silu(g) * u) @ w_out

def setup_inputs(seed: int = 0) -> dict:
    key = jax.random.key(seed)
    ks = jax.random.split(key, 18)
    f32 = jnp.float32
    nrm = lambda k, shape, scale: jax.random.normal(k, shape, f32) * scale
    return {
        'x_prompt': nrm(ks[0], (BATCH, SEQ, D_MODEL), 1.0),
        'x_sample': nrm(ks[1], (DEC_BATCH, DEC_SEQ, D_MODEL), 1.0),
        'cache_k': nrm(ks[2], (N_ATTN_LAYERS, DEC_BATCH, WINDOW, N_KV_HEADS, HEAD_DIM), 1.0),
        'cache_v': nrm(ks[3], (N_ATTN_LAYERS, DEC_BATCH, WINDOW, N_KV_HEADS, HEAD_DIM), 1.0),
        'state_gla': nrm(ks[4], (N_GLA_LAYERS, DEC_BATCH, GLA_HEADS, GLA_DK_HEAD, GLA_DV_HEAD), 1.0),
        'norm_mix': 1.0 + nrm(ks[5], (DEPTH, D_MODEL), 0.05),
        'norm_ffn': 1.0 + nrm(ks[6], (DEPTH, D_MODEL), 0.05),
        'norm_final': 1.0 + nrm(ks[7], (D_MODEL,), 0.05),
        'w_attn_in': nrm(ks[8], (N_ATTN_LAYERS, D_MODEL, Q_DIM + 2 * KV_DIM), D_MODEL ** -0.5),
        'w_attn_out': nrm(ks[9], (N_ATTN_LAYERS, Q_DIM, D_MODEL), Q_DIM ** -0.5),
        'attn_sinks': nrm(ks[10], (N_ATTN_LAYERS, N_HEADS), 0.5),
        'w_gla_in': nrm(ks[11], (N_GLA_LAYERS, D_MODEL, GLA_IN_DIM), D_MODEL ** -0.5),
        'w_gla_gate_up': nrm(ks[12], (N_GLA_LAYERS, GLA_GATE_RANK, GLA_DK), GLA_GATE_RANK ** -0.5),
        'b_gla_gate': nrm(ks[13], (N_GLA_LAYERS, GLA_DK), 0.1),
        'gla_out_norm': 1.0 + nrm(ks[14], (N_GLA_LAYERS, GLA_DV_HEAD), 0.05),
        'w_gla_out': nrm(ks[15], (N_GLA_LAYERS, GLA_DV, D_MODEL), GLA_DV ** -0.5),
        'w_ffn_in': nrm(ks[16], (DEPTH, D_MODEL, 2 * D_FF), D_MODEL ** -0.5),
        'w_ffn_out': nrm(ks[17], (DEPTH, D_FF, D_MODEL), D_FF ** -0.5),
    }

def reference(x_prompt, x_sample, cache_k, cache_v, state_gla, norm_mix, norm_ffn, norm_final,
              w_attn_in, w_attn_out, attn_sinks, w_gla_in, w_gla_gate_up, b_gla_gate, gla_out_norm,
              w_gla_out, w_ffn_in, w_ffn_out):
    yp, ys = x_prompt, x_sample
    kp_l, vp_l, sp_l, ks_l, vs_l, ss_l = [], [], [], [], [], []
    for i in range(DEPTH):
        j = i // N_MIXERS
        hp = rmsnorm(yp, norm_mix[i])
        hs = rmsnorm(ys, norm_mix[i])
        if i % N_MIXERS == 0:
            op, kp, vp = swa_prompt(hp, w_attn_in[j], w_attn_out[j], attn_sinks[j])
            os_, kn, vn = swa_sample(hs, cache_k[j], cache_v[j], w_attn_in[j], w_attn_out[j], attn_sinks[j])
            kp_l.append(kp); vp_l.append(vp); ks_l.append(kn); vs_l.append(vn)
        else:
            s0 = jnp.zeros((yp.shape[0], GLA_HEADS, GLA_DK_HEAD, GLA_DV_HEAD), jnp.float32)
            op, sp = gla_mixer(hp, s0, w_gla_in[j], w_gla_gate_up[j], b_gla_gate[j], gla_out_norm[j], w_gla_out[j])
            os_, sn = gla_mixer(hs, state_gla[j], w_gla_in[j], w_gla_gate_up[j], b_gla_gate[j], gla_out_norm[j], w_gla_out[j])
            sp_l.append(sp); ss_l.append(sn)
        yp = yp + op
        ys = ys + os_
        yp = yp + swiglu_ffn(rmsnorm(yp, norm_ffn[i]), w_ffn_in[i], w_ffn_out[i])
        ys = ys + swiglu_ffn(rmsnorm(ys, norm_ffn[i]), w_ffn_in[i], w_ffn_out[i])
    y_prompt = rmsnorm(yp, norm_final)
    y_sample = rmsnorm(ys, norm_final)
    return (y_prompt, y_sample, jnp.stack(kp_l), jnp.stack(vp_l), jnp.stack(sp_l),
            jnp.stack(ks_l), jnp.stack(vs_l), jnp.stack(ss_l))


_drawn_inputs = setup_inputs


def setup_inputs(seed=0):
    import zlib

    import numpy as np

    out = dict(_drawn_inputs(seed))
    spreads = {}
    factors = {}
    for name, (base, spread) in spreads.items():
        noise = np.random.default_rng([zlib.crc32(name.encode()), seed]).standard_normal(out[name].shape)
        drawn = base * np.exp(spread * noise) if base else spread * noise
        out[name] = __import__('jax').numpy.asarray(drawn.astype(out[name].dtype))
    for name, factor in factors.items():
        out[name] = (out[name] * factor).astype(out[name].dtype)
    return out
```

```python
from contextlib import ExitStack

import numpy as np

import concourse.bass as bass
from concourse import mybir

F32 = mybir.dt.float32
FR = mybir.dt.float32r
BF16 = mybir.dt.bfloat16
U8 = mybir.dt.uint8
WIDTH = {F32: 4, FR: 4, BF16: 2, U8: 1}
ALU = mybir.AluOpType
ACT = mybir.ActivationFunctionType

P = 128
D = 1024
KC = D // P
NP_TOK = 512
NB, NT = 8, 8
NS_TOK = NB * NT
N = NP_TOK + NS_TOK
H = N // 2
NQB = NP_TOK // P
TT = NQB + 1
WIN = 128
HD = 64
NKV, GRP = 4, 4
CTX = WIN + NT
GH, DK, DV = 4, 128, 256
CH = 64
NCH = NP_TOK // CH
FF = 2816
FC = FF // P
RANK = 16
EPS = 1e-6
NEG = -1.0e30
SLOPES = np.exp2(-8.0 * np.arange(1, NKV * GRP + 1, dtype=np.float32) / np.float32(NKV * GRP)).astype(np.float32)

B_V0, B_K, B_Q, B_O0 = 0, 2, 4, 12
B_F1 = [20, 121]
B_F2 = [64, 165]
B_VG, B_GATE, B_VG2, B_HEAD, B_O1 = 88, 92, 93, 97, 113
NBLK = 189
YS = 320
HI_PARTS = [(1, B_F1[0] + 2, True), (B_F1[0] + 2, B_F2[0] + 24, False),
            (B_F2[0] + 24, B_F1[1] + 2, True), (B_F1[1] + 2, NBLK, False)]
STAGE = 4
RING = 2
N_CONST, N_ATTC, N_GLAC = 10, 4, 4



class Tally:

    def __init__(self, sem, keys):
        self.sem = sem
        self.value = {k: i + 1 for i, k in enumerate(keys)}
        self.seen = 0

    def __getitem__(self, key):
        return self.value[key]

    def one(self, *key):
        self.seen += 1
        key = key[0] if len(key) == 1 else key
        assert self.value[key] == self.seen, (key, self.value[key], self.seen)
        return 1


class Chain:

    def __init__(self, eng, sem):
        self.eng, self.sem, self.n = eng, sem, 0

    def link(self, ins):
        self.n += 1
        ins.then_inc(self.sem, 1)
        self.eng.wait_ge(self.sem, self.n)


def tiles_in_order():
    out = [("K", 0), ("K", 1)] + [("Q", n) for n in range(8)] + [("gate", 0), ("q", 0), ("k", 0)]
    for h in range(GH):
        out += head_blocks(h)
    return out


def head_blocks(h):
    return [[("q", 1), ("k", 1), ("r", 0), ("r", 1)], [("q", 2), ("k", 2), ("r", 2), ("r", 3)],
            [("q", 3), ("k", 3), ("r", 4), ("r", 5)], [("r", 6), ("r", 7)]][h]


def gla_tensor_events():
    out = [("z", 0)]
    for h in range(GH):
        out += [("z", h + 1)] if h + 1 < GH else []
        out += [(w, h - 1) for w in ("y0", "y1", "ys")] if h else []
        out += [(w, h) for w in ("at", "ats", "ke", "kes", "u0", "u1", "u2", "u3", "o0", "o1", "os",
                                 "v0", "v1", "v2", "v3")]
    return out + [(w, GH - 1) for w in ("y0", "y1", "ys")]


def gla_vector_events():
    out = [(w, 0) for w in ("z", "la", "scan", "d1", "d2", "q1", "k1", "k2", "q2")]
    for h in range(GH):
        n = h + 1 < GH
        out += ([("yt", h - 1), ("lo", h - 1)] if h else []) + ([("z", h + 1)] if n else [])
        out += [(w, h) for w in ("at", "ats", "qm", "km")] + ([("la", h + 1), ("scan", h + 1)] if n else [])
        out += [("sa", h), ("sb", h)] + ([(w, h + 1) for w in ("d1", "d2", "q1", "k1", "k2")] if n else [])
        out += [(w, h) for w in ("v", "rs", "on")] + ([("q2", h + 1)] if n else [])
    return out + [("yt", GH - 1), ("lo", GH - 1)]


def gla_scalar_events():
    out = [(w, 0) for w in ("abs", "exp", "ln", "e1", "e2", "ek", "dec", "e3")]
    for h in range(GH):
        n = h + 1 < GH
        out += ([("hi", h - 1)] if h else []) + ([(w, h + 1) for w in ("abs", "exp", "ln")] if n else [])
        out += [("ke", h)] + ([(w, h + 1) for w in ("e1", "e2", "ek", "dec")] if n else [])
        out += [(w, h) for w in ("og", "sq", "rt")] + ([("e3", h + 1)] if n else [])
    return out + [("hi", GH - 1)]


def raw(ap):
    return ap.bitcast(F32)


def build(nc, io):
    with ExitStack() as es:
        def sem(name):
            return es.enter_context(nc.semaphore(name))

        arena = es.enter_context(nc.sbuf_tensor("arena", [P, 212800], U8))
        here = [16512]

        def at(name, off, shape, dt=F32):
            return nc.alloc_sbuf_tensor_at(name, shape, dt, offset=off)

        def take(nbytes):
            off = here[0]
            here[0] += (nbytes + 31) // 32 * 32
            return off

        def sb(name, shape, dt=F32):
            return at(name, take(int(np.prod(shape[1:])) * WIDTH[dt]), shape, dt)

        x = sb("x", [P, KC, N])
        xhi = sb("xhi", [P, KC, N], FR)
        xlo = sb("xlo", [P, KC, N], FR)
        wst = sb("wst", [P, STAGE, 1024])
        whi = sb("whi", [P, RING, 1024], FR)
        wlo = sb("wlo", [P, RING, 1024], FR)
        acc = sb("acc", [P, N])
        rbc = sb("rbc", [P, N])
        sq = sb("sq", [P, N])
        std = sq
        ident = sb("ident", [P, P])
        mean1 = sb("mean1", [P, P])
        gains = sb("gains", [P, 5, KC])
        rcol = sb("rcol", [P, 8])
        scol = sb("scol", [P, 8])
        epsz = sb("epsz", [P, 2])
        epsc, zero = epsz[:, 0:1], epsz[:, 1:2]
        sinkp = sb("sinkp", [P, 8, 2])
        sinks = sb("sinks", [P, 2])
        mx = sb("mx", [P, 2, 2])
        nm = sb("nm", [P, 2, 2])
        dn = sb("dn", [P, 2, 2])
        rd = sb("rd", [P, 2, 2])
        bm = sb("bm", [P, 4, NB])
        bgate = sb("bgate", [P, GH])
        gnorm = sb("gnorm", [P, 2])
        wup = sb("wup", [RANK, GH, P])
        km1 = sb("km1", [NS_TOK, NB])
        ss = sb("ss", [P, 2, 8])
        dcol = sb("dcol", [P, 2, 16])
        hhi_at = take(FC * N * 4)
        hlo_at = take(FC * N * 4)
        hhi = at("hhi", hhi_at, [P, FC, N], FR)
        hlo = at("hlo", hlo_at, [P, FC, N], FR)
        tail = take(12480)
        assert here[0] <= 229312, here[0]
        gs = at("gs", tail, [P, N])
        sg = at("sg", tail + 2304, [P, N])
        h32 = at("h32", tail + 4608, [P, N])
        r1, r2 = hhi_at + KC * N * 4, hlo_at + KC * N * 4
        QT = at("QT", r1, [P, 8, N])
        KT = at("KT", r1 + 18432, [P, 2, N])
        V = at("V", r1 + 23040, [P, TT, 256])
        OS = at("OS", r1 + 28160, [P, 2, 256])
        pn = at("pn", r1 + 30208, [P, 2, NB, NT])
        bias = at("bias", r2, [P, 16, 256])
        sbias = at("sbias", r2 + 16384, [P, 2, CTX])
        ktx = at("ktx", r2 + 17472, [P, 2, NB, CTX])
        PTs = at("PTs", r2 + 26176, [P, 2, 4, P])
        Vc = at("Vc", tail, [P, NB, 256])
        SC = at("SC", tail + 8192, [P, 2, 2, 260])
        silr = at("silr", hhi_at, [P, KC, N])
        QK = at("QK", hlo_at, [P, KC, N])
        VG = at("VG", r1, [P, TT, D])
        q1 = at("q1", r1 + 20480, [P, N])
        k1 = at("k1", r1 + 22784, [P, N])
        q2 = at("q2", r1 + 25088, [P, N])
        k2 = at("k2", r1 + 27392, [P, N])
        ke = at("ke", r1 + 29696, [P, TT, P])
        bb = at("bb", r2, [P, 2, N])
        t1 = at("t1", r2 + 4608, [P, N])
        t2 = at("t2", r2 + 6912, [P, N])
        AT = at("AT", r2 + 9216, [P, TT, P])
        S = at("S", r2 + 11776, [P, NCH, DV])
        qm = at("qm", r2 + 19968, [P, NB, NB, NT])
        km = at("km", r2 + 22016, [NS_TOK, NB, P])
        og = at("og", r2 + 26112, [P, TT, DV])
        rz = at("rz", tail, [P, N])
        S0 = at("S0", tail + 2304, [P, NB, DV])
        cm = at("cm", tail + 10496, [P, 4 * P], U8)
        cms = at("cms", tail + 11008, [NS_TOK, NS_TOK], U8)
        eye8 = at("eye8", tail + 11072, [P, NB, NB])
        scanm = at("scanm", tail + 11328, [P, N], BF16)
        QS = sq
        gd = sq
        junk = acc

        ps = es.enter_context(nc.psum_tensor("ps", [P, 8, 512], F32))

        s_x = [sem(f"x_loaded{c}") for c in range(KC)]
        s_gain = sem("gains_loaded")
        s_const = sem("constants_loaded")
        s_attc = sem("attention_tables_loaded")
        s_glac = sem("gla_tables_loaded")
        s_out = sem("outputs_stored")
        arrived = [sem(f"weights_arrived{i}") for i in range(STAGE)]
        zeroed = sem("zero_written")
        hi_split = sem("weights_hi_split")
        act_split = sem("weights_hi_split_by_scalar")
        w_split = sem("weights_split")
        w_used = sem("blocks_done")
        x_new, sq_done, hi_done = sem("x_updated"), sem("squares_done"), sem("x_hi_done")
        acc_done, lo_done = sem("squares_added"), sem("x_lo_done")
        norm_mm, std_done, rbc_done = sem("norm_summed"), sem("rms_done"), sem("inv_rms_done")
        tile_read = Tally(sem("tile_read"), tiles_in_order())
        g_read, u_read = [sem("g_read0"), sem("g_read1")], [sem("u_read0"), sem("u_read1")]
        silu_done = [sem("silu_done0"), sem("silu_done1")]
        h_hi, h_lo = [sem("h_hi0"), sem("h_hi1")], [sem("h_lo0"), sem("h_lo1")]
        d_mul = [sem("down_scaled0"), sem("down_scaled1")]
        y_done, s_y = sem("y_done"), sem("y_stored")
        v_chain, a_chain = sem("vector_chain"), sem("scalar_chain")
        s_ktx = sem("new_keys_placed")
        sc_done, sm_done, ex_done, pr_done = sem("scores_done"), sem("scores_biased"), sem("exp_done"), sem("probs_done")
        pt_done, pt_read, pv_done = sem("probs_turned"), sem("probs_turned_copied"), sem("pv_done")
        os_done, ot_done = sem("sample_o_copied"), sem("sample_o_turned")
        o_hi, o_lo = sem("attn_o_hi"), sem("attn_o_lo")
        silr_done = sem("silu_r_done")
        s_s0in, s_s0out, s_sp = sem("sample_states_loaded"), sem("sample_states_stored"), sem("prompt_state_stored")
        gp = Tally(sem("gla_tensor"), gla_tensor_events())
        gv = Tally(sem("gla_vector"), gla_vector_events())
        ga = Tally(sem("gla_scalar"), gla_scalar_events())
        v_read = Tally(sem("v_tiles_read"), [(part, t) for part in range(3) for t in range(TT)])

        block = es.enter_context(nc.Block())

        def pair(b):
            return ps[:, b:b + 2, 0:H]

        def cols(t, c):
            return t[:, c, :].rearrange("p (a n) -> p a n", a=2)

        def halves(t):
            return t[:, :].rearrange("p (a n) -> p a n", a=2)

        @block.sync
        def _(sp):
            w = io["w_blocks"]
            sp.dma_start(wst[:, 0, :], w[0]).then_inc(arrived[0], 16)
            for n in range(1, STAGE):
                if n == 2:
                    for c in range(2, KC):
                        sp.dma_start(x[:, c, :], io["x"][:, c, :]).then_inc(s_x[c], 16)
                sp.dma_start(wst[:, n, :], w[n]).then_inc(arrived[n], 16)
                if n == 2:
                    consts = (("epsc", epsc), ("mean1", mean1), ("ident", ident), ("sinkp", sinkp), ("sinks", sinks),
                              ("bm", bm), ("bgate", bgate), ("gnorm", gnorm), ("wup", wup), ("km1", km1))
                    assert len(consts) == N_CONST
                    for name, t in consts:
                        sp.dma_start(t[tuple(slice(None) for _ in t.shape)], io[name]).then_inc(s_const, 16)

            def load(n, slot):
                sp.wait_ge(w_split, n - (STAGE - 1))
                sp.dma_start(wst[:, slot, :], w[n]).then_inc(arrived[slot], 16)

            with sp.Fori(1, NBLK // STAGE) as r:
                for slot in range(STAGE):
                    load(r * STAGE + slot, slot)
            for n in range(NBLK // STAGE * STAGE, NBLK):
                load(n, n % STAGE)
            for c in range(KC):
                sp.wait_ge(y_done, c + 1)
                sp.dma_start(io["y"][:, c, :], x[:, c, :]).then_inc(s_y, 16)
            sp.wait_ge(s_y, 16 * KC)

        @block.gpsimd
        def _(pool):
            def split(n, slot, laps, first, own, k):
                if own:
                    pool.wait_ge(arrived[slot], 16 * laps)
                    if not first:
                        pool.wait_ge(w_used, n - (RING - 1))
                    nc.gpsimd.tensor_tensor(whi[:, slot % RING, :], wst[:, slot, :], zero[:, :].broadcast_to([P, 1024]),
                                            ALU.add).then_inc(hi_split, 1)
                pool.wait_ge(hi_split if own else act_split, k)
                nc.gpsimd.tensor_tensor(wlo[:, slot % RING, :], wst[:, slot, :], raw(whi[:, slot % RING, :]),
                                        ALU.subtract).then_inc(w_split, 1)

            nc.gpsimd.memset(zero[:, :], 0.0).then_inc(zeroed, 1)
            pool.wait_ge(zeroed, 1)
            done = {True: 0, False: 0}
            for n0, n1, own in HI_PARTS:
                k0 = done[own] + 1
                laps = (n1 - n0) // STAGE
                head = range(n0, n0 + STAGE) if n0 < STAGE else ()
                if n0 < STAGE:
                    pool.wait_ge(w_split, n0)
                for n in head:
                    split(n, n % STAGE, n // STAGE + 1, n < RING, own, k0 + n - n0)
                m0 = n0 + len(head)
                laps = (n1 - m0) // STAGE
                with pool.Fori(0, laps) as r:
                    for j in range(STAGE):
                        n = m0 + j
                        split(r * STAGE + n, n % STAGE, r + (n // STAGE + 1), False, own, r * STAGE + (k0 + n - n0))
                for n in range(m0 + laps * STAGE, n1):
                    split(n, n % STAGE, n // STAGE + 1, False, own, k0 + n - n0)
                done[own] += n1 - n0

        @block.tensor
        def _(pe):
            mm = nc.tensor.matmul

            def three(out, stat, mov, start, stop):
                mm(out, stat[0], mov[0], start=start, stop=False)
                mm(out, stat[0], mov[1], start=False, stop=False)
                return mm(out, stat[1], mov[0], start=False, stop=stop)

            def feature_block(b, slot, src, c0, nch, first, last, fresh=None, part=None):
                lo, hi = part or (0, nch)
                for c in range(lo, hi):
                    if fresh is not None:
                        pe.wait_ge(lo_done, KC * fresh + c + 1)
                    w = slice(c * P, (c + 1) * P)
                    for a in range(2):
                        s = slice(a * H, (a + 1) * H)
                        ins = three(ps[:, b + a, 0:H], (whi[:, slot, w], wlo[:, slot, w]),
                                    (src[0][:, c0 + c, s], src[1][:, c0 + c, s]),
                                    first and c == 0, last and c == nch - 1)
                return ins

            xs, hs = (xhi, xlo), (hhi, hlo)

            def tile(n, b, src, before=None):
                pe.wait_ge(w_split, n + 1)
                if before is not None:
                    pe.wait_ge(tile_read.sem, tile_read[before])
                feature_block(b, n % RING, src, 0, KC, True, True).then_inc(w_used, 1)

            def norm_sums(k, b, columns):
                if k == 0:
                    pe.wait_ge(s_const, 16 * N_CONST)
                pe.wait_ge(acc_done, KC * (k + 1))
                for a in range(2):
                    ins = mm(ps[:, b + a, 0:H], mean1[:, :], acc[:, a * H:(a + 1) * H], start=True, stop=True)
                if columns:
                    for t in range(TT):
                        m = min(P, N - t * P)
                        ins = mm(ps[0:m, 2, 2 * t:2 * t + 2], acc[:, t * P:t * P + m], mean1[:, 0:2],
                                 start=True, stop=True)
                ins.then_inc(norm_mm, 1)

            def v_blocks(n0, nblk, width, fresh=None, norm_before=None):
                per = KC // nblk
                for i in range(nblk):
                    n = n0 + i
                    pe.wait_ge(w_split, n + 1)
                    for c in range(per):
                        k = i * per + c
                        if fresh is not None:
                            pe.wait_ge(lo_done, KC * fresh + k + 1)
                        if k == norm_before:
                            norm_sums(fresh, 0, True)
                        w = slice(c * width, (c + 1) * width)
                        for t in range(TT):
                            m = min(P, N - t * P)
                            tok = slice(t * P, t * P + m)
                            ins = three(ps[0:m, 3 + t, 0:width], (xhi[:, k, tok], xlo[:, k, tok]),
                                        (whi[:, n % RING, w], wlo[:, n % RING, w]), k == 0, k == KC - 1)
                    ins.then_inc(w_used, 1)

            v_blocks(B_V0, 2, 256, fresh=0, norm_before=KC - 1)
            pe.wait_ge(std_done, 1)
            tile(B_K, 0, xs)
            pe.wait_ge(v_read.sem, v_read[0, 0])
            tile(B_K + 1, 2, xs)
            tile(B_Q, 0, xs, before=("K", 0))
            pe.wait_ge(v_read.sem, v_read[0, TT - 1])
            pe.wait_ge(tile_read.sem, tile_read["K", 1])

            def scores(s):
                par = s % 2
                if s >= 2:
                    pe.wait_ge(sm_done, s - 1)
                if s < 32:
                    n, i = divmod(s, NQB)
                    pe.wait_ge(tile_read.sem, tile_read["Q", n])
                    k0 = (i - 1) * P if i else 0
                    c0 = 0 if i else P
                    for hd in range(2):
                        q = slice(HD * hd, HD * hd + HD)
                        ins = mm(ps[:, 3 + 2 * par + hd, c0:256], QT[q, n, i * P:(i + 1) * P],
                                 KT[q, n // GRP, k0:(i + 1) * P], start=True, stop=True)
                else:
                    pb, e = divmod(s - 32, 2)
                    if s == 32:
                        pe.wait_ge(tile_read.sem, tile_read["Q", 7])
                        pe.wait_ge(s_ktx, 3)
                    q = slice(HD * e, HD * e + HD)
                    for b2 in range(2):
                        b = 2 * pb + b2
                        for gg in range(2):
                            r = 32 * (2 * b2 + gg)
                            c = 32 * (NB * gg + b)
                            ins = mm(ps[r:r + 32, 3 + 2 * par, 0:CTX], QS[q, c:c + 32],
                                     ktx[q, gg, b, :], start=True, stop=True)
                ins.then_inc(sc_done, 1)

            def turn(s):
                par = s % 2
                pe.wait_ge(pr_done, s + 1)
                if s >= 1:
                    pe.wait_ge(pt_read, s)
                if s < 32:
                    for hd in range(2):
                        for kc in range(0 if s % NQB else 1, 2):
                            ins = mm(ps[:, 7, (2 * hd + kc) * P:(2 * hd + kc + 1) * P],
                                     SC[:, par, hd, kc * P:(kc + 1) * P], ident[:, :], start=True, stop=True,
                                     is_transpose=True)
                else:
                    mm(ps[:, 7, 0:P], SC[:, par, 0, 0:P], ident[:, :], start=True, stop=True, is_transpose=True)
                    ins = mm(ps[0:NS_TOK, 7, P:2 * P], pn[:, par, :, :], ident[:, :],
                             start=True, stop=True, is_transpose=True)
                ins.then_inc(pt_done, 1)

            def values(s):
                par = s % 2
                pe.wait_ge(pt_read, s + 1)
                if s < 32:
                    n, i = divmod(s, NQB)
                    if i == 0 and n >= 1:
                        pe.wait_ge(o_lo, n)
                    for hd in range(2):
                        g = 2 * (n // GRP) + hd
                        for kc in range(0 if i else 1, 2):
                            ins = mm(ps[HD * hd:HD * hd + HD, 2, i * P:(i + 1) * P],
                                     V[:, i - 1 + kc, g * HD:(g + 1) * HD], PTs[:, par, 2 * hd + kc, :],
                                     start=(kc == 0 or i == 0), stop=(kc == 1))
                else:
                    pe.wait_ge(o_lo, 8) if s == 32 else pe.wait_ge(os_done, s - 32)
                    pb = (s - 32) // 2
                    for b2 in range(2):
                        mm(ps[64 * b2:64 * b2 + 64, 2, 0:256], PTs[:, par, 0, 64 * b2:64 * b2 + 64],
                           Vc[:, 2 * pb + b2, :], start=True, stop=False)
                    ins = mm(ps[:, 2, 0:256], PTs[0:NS_TOK, par, 1, :], V[0:NS_TOK, NQB, :], start=False, stop=True)
                ins.then_inc(pv_done, 1)

            def turn_out(s):
                par = s % 2
                pe.wait_ge(os_done, s - 31)
                if s >= 34:
                    pe.wait_ge(o_lo, 8 + s - 33)
                for t in range(2):
                    ins = mm(ps[:, par, t * P:(t + 1) * P], OS[:, par, t * P:(t + 1) * P], ident[:, :],
                             start=True, stop=True, is_transpose=True)
                ins.then_inc(ot_done, 1)

            for s in range(43):
                n, i = divmod(s, NQB)
                if n + 1 < 8:
                    blk = B_Q + n + 1
                    if i == 0:
                        pe.wait_ge(w_split, blk + 1)
                        pe.wait_ge(tile_read.sem, tile_read["Q", n])
                    ins = feature_block(0, blk % RING, xs, 0, KC, True, True, part=(2 * i, 2 * i + 2))
                    if i == NQB - 1:
                        ins.then_inc(w_used, 1)
                if s < 40:
                    scores(s)
                if 1 <= s < 41:
                    turn(s - 1)
                if 2 <= s < 42:
                    values(s - 2)
                if s >= 35:
                    turn_out(s - 3)

            pe.wait_ge(o_lo, 16)
            for m in range(KC):
                if m >= 2:
                    pe.wait_ge(x_new, m - 1)
                tile(B_O0 + m, 2 * (m % 2), hs)

            def ffn(l):
                k = 2 * l + 1
                pe.wait_ge(w_split, B_F1[l] + 1)
                pe.wait_ge(x_new, KC * k - 1)
                feature_block(0, B_F1[l] % RING, xs, 0, KC, True, True, fresh=k).then_inc(w_used, 1)
                norm_sums(k, 4, False)
                pe.wait_ge(w_split, B_F1[l] + 2)
                pe.wait_ge(x_new, KC * k)
                feature_block(2, (B_F1[l] + 1) % RING, xs, 0, KC, True, True).then_inc(w_used, 1)
                with pe.Fori(1, FC) as f:
                    for u in range(2):
                        pe.wait_ge(w_split, f * 2 + (B_F1[l] + u + 1))
                        pe.wait_ge([g_read, u_read][u][l], f)
                        feature_block(2 * u, (B_F1[l] + u) % RING, xs, 0, KC, True, True).then_inc(w_used, 1)

                def down(m, odd, first):
                    if first:
                        pe.wait_ge([g_read, u_read][odd][l], FC)
                    else:
                        pe.wait_ge(d_mul[l], m - 1)
                    for j, nch in enumerate((8, 8, 6)):
                        n = m * 3 + (B_F2[l] + j)
                        pe.wait_ge(w_split, n + 1)
                        if first and not odd and j == 0:
                            pe.wait_ge(h_lo[l], FC - 1)
                        if first and not odd and j == 2:
                            pe.wait_ge(h_lo[l], FC)
                        feature_block(2 * odd, (B_F2[l] + 3 * odd + j) % RING, hs, 8 * j, nch, j == 0,
                                      j == 2).then_inc(w_used, 1)

                for m in range(2):
                    down(m, m, True)
                with pe.Fori(1, KC // 2) as r:
                    for odd in range(2):
                        down(r * 2 + odd, odd, False)

            ffn(0)

            pe.wait_ge(x_new, 16)
            v_blocks(B_VG, 4, 512, fresh=2, norm_before=6)
            pe.wait_ge(std_done, 3)
            tile(B_GATE, 0, xs)
            pe.wait_ge(v_read.sem, v_read[1, TT - 1])
            v_blocks(B_VG2, 4, 512)
            tile(B_HEAD, 0, xs, before=("gate", 0))
            pe.wait_ge(v_read.sem, v_read[2, TT - 1])

            def gate_pre(h):
                if h == 0:
                    pe.wait_ge(s_glac, 16 * N_GLAC)
                else:
                    pe.wait_ge(gv.sem, gv["on", h - 2] if h > 1 else gv["z", 0])
                for a in range(2):
                    ins = mm(ps[:, 4 + a, 0:H], wup[:, h, :], gd[0:RANK, a * H:(a + 1) * H], start=True, stop=True)
                ins.then_inc(gp.sem, gp.one("z", h))

            def scores_and_keys(h):
                pe.wait_ge(gv.sem, gv["k2", h])
                if h + 1 < GH:
                    pe.wait_ge(gv.sem, gv["z", h + 1])
                else:
                    pe.wait_ge(gv.sem, gv["yt", h - 1])
                for t in range(NQB):
                    ts = slice(t * P, (t + 1) * P)
                    ins = mm(ps[:, 6, ts], k1[:, ts], q1[:, ts], start=True, stop=True)
                ins.then_inc(gp.sem, gp.one("at", h))
                mm(ps[0:NS_TOK, 7, 0:NS_TOK], k1[:, NP_TOK:N], q1[:, NP_TOK:N], start=True,
                   stop=True).then_inc(gp.sem, gp.one("ats", h))
                for t in range(NQB):
                    ts = slice(t * P, (t + 1) * P)
                    ins = mm(ps[:, 4, ts], k2[:, ts], ident[:, :], start=True, stop=True, is_transpose=True)
                ins.then_inc(gp.sem, gp.one("ke", h))
                mm(ps[0:NS_TOK, 5, 0:P], k2[:, NP_TOK:N], ident[:, :], start=True, stop=True,
                   is_transpose=True).then_inc(gp.sem, gp.one("kes", h))

            def state_updates(h):
                pe.wait_ge(ga.sem, ga["ke", h])
                pe.wait_ge(gv.sem, gv["ats", h])
                for u, (b, c) in enumerate(((6, 0), (7, 1), (4, 4), (5, 5))):
                    for i in range(2):
                        r = slice(CH * (c % 2), CH * (c % 2) + CH)
                        ins = mm(ps[:, b, i * DV:(i + 1) * DV], ke[r, (c + 2 * i) // 2, :],
                                 VG[r, (c + 2 * i) // 2, h * DV:(h + 1) * DV], start=True, stop=True)
                    ins.then_inc(gp.sem, gp.one(f"u{u}", h))

            def outputs(h):
                pe.wait_ge(gv.sem, gv["sb", h])
                for o in range(2):
                    for i in range(2):
                        t = 2 * o + i
                        out = slice(i * DV, (i + 1) * DV)
                        mm(ps[:, 6 + o, out], AT[:, t, :], VG[:, t, h * DV:(h + 1) * DV], start=True,
                           stop=False, skip_group_check=True)
                        for c in (2 * t, 2 * t + 1):
                            if c:
                                r = slice(CH * (c % 2), CH * (c % 2) + CH)
                                ins = mm(ps[r, 6 + o, out], q2[:, c * CH:(c + 1) * CH], S[:, c - 1, :],
                                         start=False, stop=True, skip_group_check=True)
                    ins.then_inc(gp.sem, gp.one(f"o{o}", h))
                pe.wait_ge(gv.sem, gv["qm", h])
                pe.wait_ge(s_s0in, 16 * (h + 1))
                mm(ps[0:NS_TOK, 4, 0:DV], AT[0:NS_TOK, NQB, 0:NS_TOK],
                   VG[0:NS_TOK, NQB, h * DV:(h + 1) * DV], start=True, stop=False)
                for b in range(NB):
                    ins = mm(ps[0:NS_TOK, 4, 0:DV], qm[:, b, :, :], S0[:, b, :], start=False,
                             stop=(b == NB - 1))
                ins.then_inc(gp.sem, gp.one("os", h))

            def sequence_updates(h):
                pe.wait_ge(gv.sem, gv["km", h])
                for i, b in enumerate((5, 6, 7, 4)):
                    if i == 1:
                        pe.wait_ge(ga.sem, ga["og", h])
                    for e in range(2):
                        ins = mm(ps[:, b, e * DV:(e + 1) * DV], km[:, 2 * i + e, :],
                                 VG[0:NS_TOK, NQB, h * DV:(h + 1) * DV], start=True, stop=True)
                    ins.then_inc(gp.sem, gp.one(f"v{i}", h))

            def turn_outputs(h):
                pe.wait_ge(gv.sem, gv["on", h])
                for d in range(2):
                    for t in range(NQB):
                        ins = mm(ps[:, 6 + d, t * P:(t + 1) * P], og[:, t, d * P:(d + 1) * P], ident[:, :],
                                 start=True, stop=True, is_transpose=True)
                    ins.then_inc(gp.sem, gp.one(f"y{d}", h))
                for d in range(2):
                    ins = mm(ps[:, 5, YS + d * NS_TOK:YS + (d + 1) * NS_TOK], og[0:NS_TOK, NQB, d * P:(d + 1) * P],
                             ident[0:NS_TOK, 0:NS_TOK], start=True, stop=True, is_transpose=True)
                ins.then_inc(gp.sem, gp.one("ys", h))

            gate_pre(0)
            tile(B_HEAD + 1, 2, xs)
            last_in = {0: ("q", 0), 2: ("k", 0)}
            blk = B_HEAD + 2

            def project_out(m, c0, c1):
                if c0 == 0:
                    pe.wait_ge(w_split, B_O1 + m + 1)
                    pe.wait_ge(tile_read.sem, tile_read[last_in[2 * m]])
                pe.wait_ge(gv.sem, gv["lo", (c1 - 1) // 2])
                ins = feature_block(2 * m, (B_O1 + m) % RING, hs, 0, KC, True, True, part=(c0, c1))
                if c1 == KC:
                    ins.then_inc(w_used, 1)

            for h in range(GH):
                ahead = head_blocks(h)
                for j in range(4):
                    if j < len(ahead):
                        b = 2 * (j % 2)
                        tile(blk, b, xs, before=last_in[b])
                        last_in[b] = ahead[j]
                        blk += 1
                    if h == GH - 1 and j >= 2:
                        project_out(0, *((0, 2), (2, 6))[j - 2])
                    if j == 0:
                        if h + 1 < GH:
                            gate_pre(h + 1)
                        if h:
                            turn_outputs(h - 1)
                    if j == 1:
                        scores_and_keys(h)
                    if j == 2:
                        state_updates(h)
                    if j == 3:
                        outputs(h)
                        sequence_updates(h)
            project_out(1, 0, 4)
            turn_outputs(GH - 1)
            project_out(1, 4, 6)

            for m in range(2):
                project_out(m, 6, KC)
            for m in range(2, KC):
                pe.wait_ge(x_new, 2 * KC + m - 1)
                tile(B_O1 + m, 2 * (m % 2), hs)
            ffn(1)
            norm_sums(4, 4, False)

        @block.vector
        def _(dve):
            chain = Chain(dve, v_chain)
            tt, ts, stt = nc.vector.tensor_tensor, nc.vector.tensor_scalar, nc.vector.scalar_tensor_tensor

            def at_chunk(m):
                return m if isinstance(m, int) else bass.ds(m, 1)

            def chunk(t, m):
                return t[:, m, :] if isinstance(m, int) else t[:, bass.ds(m, 1), :]

            def gain(k, m):
                return gains[:, k, m:m + 1] if isinstance(m, int) else gains[:, k, bass.ds(m, 1)]

            def prepare(k, m, first=False):
                if k < 4:
                    dve.wait_ge(hi_done, m + (KC * k + 1))
                    stt(chunk(xlo, m), chunk(x, m), gain(k, m), raw(chunk(xhi, m)), ALU.mult,
                        ALU.subtract).then_inc(lo_done, 1)
                dve.wait_ge(sq_done, m + (KC * k + 1))
                if first:
                    if k:
                        dve.wait_ge(norm_mm, k)
                    nc.vector.tensor_copy(acc[:, :], sq[:, :]).then_inc(acc_done, 1)
                else:
                    dve.wait_ge(acc_done, m + KC * k)
                    tt(acc[:, :], acc[:, :], sq[:, :], ALU.add).then_inc(acc_done, 1)

            def inv_rms(k, columns):
                dve.wait_ge(std_done, k + 1)
                ins = nc.vector.reciprocal(rbc[:, :], std[:, :])
                if columns:
                    nc.vector.reciprocal(rcol[:, 0:NQB], scol[:, 0:NQB])
                    ins = nc.vector.reciprocal(rcol[0:NS_TOK, NQB:TT], scol[0:NS_TOK, NQB:TT])
                ins.then_inc(rbc_done, 1)
                dve.wait_ge(rbc_done, k + 1)

            def read_values(part, last_block, dst, c0, width):
                dve.wait_ge(w_used, last_block + 1)
                for t in range(TT):
                    m = min(P, N - t * P)
                    ts(dst[0:m, t, c0:c0 + width], ps[0:m, 3 + t, 0:width], rcol[0:m, t:t + 1], None,
                       ALU.mult).then_inc(v_read.sem, v_read.one(part, t))

            def read_tile(key, n, b, dst, scale=None):
                dve.wait_ge(w_used, n + 1)
                ins = (tt(dst, pair(b), halves(rbc), ALU.mult) if scale is None else
                       stt(dst, pair(b), scale, halves(rbc), ALU.mult, ALU.mult))
                ins.then_inc(tile_read.sem, tile_read.one(*key))

            dve.wait_ge(arrived[0], 16)
            chain.link(nc.vector.tensor_copy(whi[:, 0, :], wst[:, 0, :]))
            tt(wlo[:, 0, :], wst[:, 0, :], raw(whi[:, 0, :]), ALU.subtract).then_inc(w_split, 1)
            dve.wait_ge(s_gain, 16)
            for m in range(KC):
                dve.wait_ge(s_x[m], 16)
                prepare(0, m, m == 0)
            dve.wait_ge(s_const, 16 * N_CONST)
            inv_rms(0, True)
            read_values(0, B_V0 + 1, V, 0, 256)
            for t in range(2):
                read_tile(("K", t), B_K + t, 2 * t, cols(KT, t))
            dve.wait_ge(s_attc, 16 * N_ATTC)
            dve.wait_ge(tile_read.sem, tile_read["K", 1])
            nc.vector.tensor_copy(ktx[:, :, :, WIN:CTX],
                                  KT[:, :, NP_TOK:N].rearrange("p t (b k) -> p t b k", b=NB)).then_inc(s_ktx, 1)
            read_tile(("Q", 0), B_Q, 0, cols(QT, 0), HD ** -0.5)

            def biased(s):
                par = s % 2
                if s >= 2:
                    dve.wait_ge(pt_done, s - 1)
                if s < 32:
                    n, i = divmod(s, NQB)
                    c0 = 0 if i else P
                    nc.vector.tensor_copy(SC[:, par, :, 256:257], sinkp[:, n, :].unsqueeze(2))
                    dve.wait_ge(sc_done, s + 1)
                    for hd in range(2):
                        ins = nc.vector.tensor_tensor_reduce(
                            SC[:, par, hd, c0:256], ps[:, 3 + 2 * par + hd, c0:256], bias[:, 2 * n + hd, c0:256],
                            1.0, sinkp[:, n, hd:hd + 1], ALU.add, ALU.max, mx[:, par, hd:hd + 1])
                    chain.link(ins)
                    ts(nm[:, par, :], mx[:, par, :], -1.0, None, ALU.mult).then_inc(sm_done, 1)
                else:
                    e = s % 2
                    nc.vector.tensor_copy(SC[:, par, 0, CTX:CTX + 1], sinks[:, e:e + 1])
                    dve.wait_ge(sc_done, s + 1)
                    chain.link(nc.vector.tensor_tensor_reduce(
                        SC[:, par, 0, 0:CTX], ps[:, 3 + 2 * par, 0:CTX], sbias[:, e, :],
                        1.0, sinks[:, e:e + 1], ALU.add, ALU.max, mx[:, par, 0:1]))
                    ts(nm[:, par, 0:1], mx[:, par, 0:1], -1.0, None, ALU.mult).then_inc(sm_done, 1)

            def probs(s):
                par = s % 2
                dve.wait_ge(ex_done, s + 1)
                if s < 32:
                    c0 = 0 if s % NQB else P
                    chain.link(nc.vector.reciprocal(rd[:, par, :], dn[:, par, :]))
                    for hd in range(2):
                        ins = ts(SC[:, par, hd, c0:256], SC[:, par, hd, c0:256], rd[:, par, hd:hd + 1], None, ALU.mult)
                    ins.then_inc(pr_done, 1)
                else:
                    chain.link(nc.vector.reciprocal(rd[:, par, 0:1], dn[:, par, 0:1]))
                    chain.link(ts(SC[:, par, 0, 0:CTX], SC[:, par, 0, 0:CTX], rd[:, par, 0:1], None, ALU.mult))
                    tt(pn[:, par, :, :], SC[:, par, 0, WIN:CTX].unsqueeze(1).to_broadcast([P, NB, NT]),
                       bm[:, (s - 32) // 2, :].unsqueeze(2).to_broadcast([P, NB, NT]), ALU.mult).then_inc(pr_done, 1)

            def sample_views(s, t):
                e, pb = s % 2, (s - 32) // 2
                q = slice(HD * e, HD * e + HD)
                src = ps[q, s % 2, t * P:(t + 1) * P].rearrange("p (b g j k) -> p g b j k", b=2, g=2, j=GRP)[:, t]
                tok = slice(NP_TOK + 2 * NT * pb, NP_TOK + 2 * NT * (pb + 1))
                return src, [o[q, GRP * t:GRP * (t + 1), tok].rearrange("p j (b k) -> p b j k", b=2)
                             for o in (hhi, hlo)]

            for s in range(43):
                n, i = divmod(s, NQB)
                if n + 1 < 8 and i == NQB - 1:
                    read_tile(("Q", n + 1), B_Q + n + 1, 0, cols(QT, n + 1), HD ** -0.5)
                    if (n + 1) % GRP == GRP - 1:
                        t = (n + 1) // GRP
                        dve.wait_ge(tile_read.sem, tile_read["Q", n + 1])
                        for b in range(NB):
                            tok = slice(NP_TOK + b * NT, NP_TOK + (b + 1) * NT)
                            c = 32 * (NB * t + b)
                            ins = nc.vector.tensor_copy(QS[:, c:c + 32].rearrange("p (j k) -> p j k", j=GRP),
                                                        QT[:, GRP * t:GRP * (t + 1), tok])
                        ins.then_inc(s_ktx, 1)
                if s < 40:
                    biased(s)
                    probs(s)
                if s >= 5 and (s - 5) % NQB == 0 and (s - 5) // NQB < 8:
                    n = (s - 5) // NQB
                    dve.wait_ge(o_hi, n + 1)
                    tt(hlo[:, n, 0:NP_TOK], ps[:, 2, :], raw(hhi[:, n, 0:NP_TOK]), ALU.subtract).then_inc(o_lo, 1)
                if s >= 34 and s < 42:
                    dve.wait_ge(pv_done, s - 1)
                    if s >= 36:
                        dve.wait_ge(ot_done, s - 35)
                    nc.vector.tensor_copy(OS[:, s % 2, :], ps[:, 2, 0:256]).then_inc(os_done, 1)
                if s >= 35:
                    dve.wait_ge(o_hi, 8 + s - 34)
                    for t in range(2):
                        src, (hi, lo) = sample_views(s - 3, t)
                        ins = tt(lo, src, raw(hi), ALU.subtract)
                    ins.then_inc(o_lo, 1)

            def add_projection(b0, k, m):
                dve.wait_ge(w_used, b0 + m + 1)
                tt(cols(x, m), pair(2 * (m % 2)), cols(x, m), ALU.add).then_inc(x_new, 1)
                prepare(k, m, m == 0)

            for m in range(KC):
                add_projection(B_O0, 1, m)

            def ffn(l):
                k = 2 * l + 1
                inv_rms(k, False)

                def hidden(f, first):
                    dve.wait_ge(w_used, f * 2 + (B_F1[l] + 1))
                    if not first:
                        dve.wait_ge(silu_done[l], f)
                    tt(halves(gs), pair(0), halves(rbc), ALU.mult).then_inc(g_read[l], 1)
                    dve.wait_ge(w_used, f * 2 + (B_F1[l] + 2))
                    dve.wait_ge(silu_done[l], f + 1)
                    tt(halves(h32), pair(2), halves(sg), ALU.mult).then_inc(u_read[l], 1)
                    dve.wait_ge(h_hi[l], f + 1)
                    tt(chunk(hlo, f), h32[:, :], raw(chunk(hhi, f)), ALU.subtract).then_inc(h_lo[l], 1)

                hidden(0, True)
                with dve.Fori(1, FC) as f:
                    hidden(f, False)

                def down(m, odd, first):
                    dve.wait_ge(w_used, m * 3 + (B_F2[l] + 3))
                    tt(halves(gs), pair(2 * odd), halves(rbc), ALU.mult).then_inc(d_mul[l], 1)
                    dve.wait_ge(d_mul[l], m + 1)
                    tt(chunk(x, m), gs[:, :], chunk(x, m), ALU.add).then_inc(x_new, 1)
                    prepare(k + 1, m, first and not odd)

                for m in range(2):
                    down(m, m, True)
                with dve.Fori(1, KC // 2) as r:
                    for odd in range(2):
                        down(r * 2 + odd, odd, False)

            ffn(0)

            chain.link(nc.vector.memset(AT[:, :, :], 0.0))
            inv_rms(2, True)
            read_values(1, B_GATE - 1, VG, 0, 512)
            dve.wait_ge(w_used, B_GATE + 1)
            tt(gd[0:RANK, :].rearrange("p (a n) -> p a n", a=2), ps[0:RANK, 0:2, 0:H],
               rbc[0:RANK, :].rearrange("p (a n) -> p a n", a=2),
               ALU.mult).then_inc(tile_read.sem, tile_read.one("gate", 0))
            read_values(2, B_HEAD - 1, VG, 512, 512)
            dve.wait_ge(s_glac, 16 * N_GLAC)
            nc.vector.tensor_copy(cm[:, :], q1[:, 0:NQB * P])
            nc.vector.tensor_copy(cms[:, :], k1[0:NS_TOK, 0:NS_TOK])
            chain.link(nc.vector.tensor_copy(scanm[:, :], q2[:, :]))

            def prompt_view(t):
                return t[:, 0:NP_TOK].rearrange("p (c k) -> p c k", k=CH)

            def sample_view(t):
                return t[:, NP_TOK:N].rearrange("p (c k) -> p c k", k=NT)

            def sig(ins, key, h):
                ins.then_inc(gv.sem, gv.one(key, h))

            def gates(h):
                dve.wait_ge(gp.sem, gp["z", h])
                if h >= 2:
                    dve.wait_ge(gv.sem, gv["lo", h - 2])
                ts(halves(t1), pair(4), bgate[:, h:h + 1], None, ALU.add).then_inc(gv.sem, gv.one("z", h))

            def decay(h):
                dve.wait_ge(ga.sem, ga["ln", h])
                stt(t1[:, :], t1[:, :], 0.0, t2[:, :], ALU.min, ALU.subtract).then_inc(gv.sem, gv.one("la", h))
                dve.wait_ge(gv.sem, gv["la", h])
                nc.vector.tensor_tensor_scan(bb[:, h % 2, :], scanm[:, :], t1[:, :], 0.0, ALU.mult,
                                             ALU.add).then_inc(gv.sem, gv.one("scan", h))

            def decayed(h):
                b = bb[:, h % 2, :]
                dve.wait_ge(gv.sem, gv["scan", h])
                for view, k in ((prompt_view, CH), (sample_view, NT)):
                    ins = tt(view(t1), view(b), view(b)[:, :, k // 2:k // 2 + 1].to_broadcast([P, 8, k]), ALU.subtract)
                ins.then_inc(gv.sem, gv.one("d1", h))
                for view, k in ((prompt_view, CH), (sample_view, NT)):
                    ins = tt(view(t2), view(b)[:, :, k - 1:k].to_broadcast([P, 8, k]), view(b), ALU.subtract)
                ins.then_inc(gv.sem, gv.one("d2", h))
                dve.wait_ge(tile_read.sem, tile_read["k", h])
                dve.wait_ge(ga.sem, ga["e1", h])
                tt(q1[:, :], q1[:, :], QK[:, 2 * h, :], ALU.mult).then_inc(gv.sem, gv.one("q1", h))
                dve.wait_ge(ga.sem, ga["e2", h])
                tt(k1[:, :], k1[:, :], QK[:, 2 * h + 1, :], ALU.mult).then_inc(gv.sem, gv.one("k1", h))
                dve.wait_ge(ga.sem, ga["ek", h])
                tt(k2[:, :], k2[:, :], QK[:, 2 * h + 1, :], ALU.mult).then_inc(gv.sem, gv.one("k2", h))

            def carried(h):
                dve.wait_ge(ga.sem, ga["e3", h])
                tt(q2[:, :], q2[:, :], QK[:, 2 * h, :], ALU.mult).then_inc(gv.sem, gv.one("q2", h))

            def read_block(key, n, b):
                kind, i = key
                if kind == "q":
                    read_tile(key, n, b, cols(QK, 2 * i), DK ** -0.5)
                elif kind == "k":
                    read_tile(key, n, b, cols(QK, 2 * i + 1))
                else:
                    if i:
                        dve.wait_ge(silr_done, i)
                    read_tile(key, n, b, halves(rz))

            read_block(("q", 0), B_HEAD, 0)
            gates(0)
            read_block(("k", 0), B_HEAD + 1, 2)
            decay(0)
            decayed(0)
            carried(0)
            def turned_outputs(h):
                dve.wait_ge(silr_done, 2 * h + 2)
                dve.wait_ge(gp.sem, gp["ys", h])
                for d, y in enumerate((t1, t2)):
                    stt(y[:, 0:NP_TOK], ps[:, 6 + d, :], gnorm[:, d:d + 1], silr[:, 2 * h + d, 0:NP_TOK],
                        ALU.mult, ALU.mult)
                    ins = stt(y[:, NP_TOK:N], ps[:, 5, YS + d * NS_TOK:YS + (d + 1) * NS_TOK], gnorm[:, d:d + 1],
                              silr[:, 2 * h + d, NP_TOK:N], ALU.mult, ALU.mult)
                sig(ins, "yt", h)
                dve.wait_ge(ga.sem, ga["hi", h])
                for d, y in enumerate((t1, t2)):
                    ins = tt(hlo[:, 2 * h + d, :], y[:, :], raw(hhi[:, 2 * h + d, :]), ALU.subtract)
                sig(ins, "lo", h)

            def masked_scores(h):
                if h:
                    dve.wait_ge(gp.sem, gp["os", h - 1])
                dve.wait_ge(gp.sem, gp["at", h])
                sig(nc.vector.copy_predicated(AT[:, 0:NQB, :], cm[:, :].rearrange("p (t k) -> p t k", k=P),
                                              ps[:, 6, :].rearrange("p (t k) -> p t k", k=P)), "at", h)
                dve.wait_ge(gp.sem, gp["ats", h])
                sig(nc.vector.copy_predicated(AT[0:NS_TOK, NQB, 0:NS_TOK], cms[:, :],
                                              ps[0:NS_TOK, 7, 0:NS_TOK]), "ats", h)

            def by_sequence(h):
                dve.wait_ge(gv.sem, gv["q2", h])
                sig(tt(qm[:, :, :, :], sample_view(q2).unsqueeze(1).to_broadcast([P, NB, NB, NT]),
                       eye8[:, :, :].unsqueeze(3).to_broadcast([P, NB, NB, NT]), ALU.mult), "qm", h)
                if h:
                    dve.wait_ge(gp.sem, gp["v3", h - 1])
                dve.wait_ge(ga.sem, ga["ke", h])
                sig(tt(km[:, :, :], ke[0:NS_TOK, NQB, :].unsqueeze(1).to_broadcast([NS_TOK, NB, P]),
                       km1[:, :].unsqueeze(2).to_broadcast([NS_TOK, NB, P]), ALU.mult), "km", h)

            def states(h):
                if h:
                    dve.wait_ge(s_sp, 16 * h)
                for c in range(NCH):
                    bk = ((6, 7), (4, 5))[c // 4][c % 2]
                    u = ps[:, bk, (c // 2 % 2) * DV:(c // 2 % 2 + 1) * DV]
                    if c % 4 == 0:
                        dve.wait_ge(gp.sem, gp[("u1", "u3")[c // 4], h])
                    if c == 0:
                        ins = nc.vector.tensor_copy(S[:, 0, :], u)
                    else:
                        ins = stt(S[:, c, :], S[:, c - 1, :], dcol[:, h % 2, c:c + 1], u, ALU.mult, ALU.add)
                    if c == 3:
                        sig(ins, "sa", h)
                        dve.wait_ge(gv.sem, gv["sa", h])
                    elif c == 7:
                        sig(ins, "sb", h)
                    else:
                        chain.link(ins)

            def sequence_states(h):
                dve.wait_ge(gp.sem, gp["v3", h])
                for b in range(NB):
                    ins = stt(S0[:, b, :], S0[:, b, :], dcol[:, h % 2, 8 + b:9 + b],
                              ps[:, (5, 6, 7, 4)[b // 2], (b % 2) * DV:(b % 2 + 1) * DV], ALU.mult, ALU.add)
                sig(ins, "v", h)

            def normed(h):
                dve.wait_ge(ga.sem, ga["rt", h])
                nc.vector.reciprocal(ss[:, 1, 0:NQB], ss[:, 1, 0:NQB])
                sig(nc.vector.reciprocal(ss[0:NS_TOK, 1, NQB:TT], ss[0:NS_TOK, 1, NQB:TT]), "rs", h)
                dve.wait_ge(gv.sem, gv["rs", h])
                for t in range(TT):
                    m = P if t < NQB else NS_TOK
                    ins = ts(og[0:m, t, :], og[0:m, t, :], ss[0:m, 1, t:t + 1], None, ALU.mult)
                sig(ins, "on", h)

            blk = B_HEAD + 2
            for h in range(GH):
                ahead = head_blocks(h)
                nxt = h + 1 < GH
                for j in range(4):
                    if j < len(ahead):
                        read_block(ahead[j], blk, 2 * (j % 2))
                        blk += 1
                    if j == 0:
                        if h:
                            turned_outputs(h - 1)
                        if nxt:
                            gates(h + 1)
                    if j == 1:
                        masked_scores(h)
                        by_sequence(h)
                        if nxt:
                            decay(h + 1)
                    if j == 2:
                        states(h)
                        if nxt:
                            decayed(h + 1)
                    if j == 3:
                        sequence_states(h)
                        normed(h)
                        if nxt:
                            carried(h + 1)
            turned_outputs(GH - 1)

            for m in range(KC):
                add_projection(B_O1, 3, m)
            ffn(1)

            inv_rms(4, False)
            for m in range(KC):
                stt(x[:, m, :], x[:, m, :], gains[:, 4, m:m + 1], rbc[:, :], ALU.mult, ALU.mult).then_inc(y_done, 1)

        @block.scalar
        def _(act):
            chain = Chain(act, a_chain)
            fn = nc.scalar.activation

            def chunk(t, m):
                return t[:, m, :] if isinstance(m, int) else t[:, bass.ds(m, 1), :]

            def gain(k, m):
                return gains[:, k, m:m + 1] if isinstance(m, int) else gains[:, k, bass.ds(m, 1)]

            def prepare(k, m, first=False):
                if k:
                    act.wait_ge(x_new, m + (KC * (k - 1) + 1))
                if k < 4:
                    fn(chunk(xhi, m), chunk(x, m), ACT.Copy, scale=gain(k, m)).then_inc(hi_done, 1)
                if k or not first:
                    act.wait_ge(acc_done, m + KC * k)
                fn(sq[:, :] if isinstance(m, int) else sq[:, :].unsqueeze(1), chunk(x, m),
                   ACT.Square).then_inc(sq_done, 1)

            def rms(k, b, columns):
                act.wait_ge(norm_mm, k + 1)
                ins = fn(halves(std), pair(b), ACT.Sqrt, bias=epsc[:, :])
                if columns:
                    fn(scol[:, 0:NQB], ps[:, 2, 0:2 * NQB].rearrange("p (t e) -> p t e", e=2)[:, :, 0], ACT.Sqrt,
                       bias=epsc[:, :])
                    ins = fn(scol[0:NS_TOK, NQB:TT], ps[0:NS_TOK, 2, 2 * NQB:2 * NQB + 1], ACT.Sqrt,
                             bias=epsc[0:NS_TOK, :])
                ins.then_inc(std_done, 1)

            act.dma_start(gains[:, :, :], io["gains"]).then_inc(s_gain, 16)
            for c in range(2):
                act.dma_start(x[:, c, :], io["x"][:, c, :]).then_inc(s_x[c], 16)
            act.wait_ge(s_gain, 16)
            for m in range(KC):
                act.wait_ge(s_x[m], 16)
                prepare(0, m, m == 0)
            act.wait_ge(s_const, 16 * N_CONST)
            rms(0, 0, True)
            for dst, name in ((ktx[:, :, :, 0:WIN], "ktx"), (bias[:, :, :], "bias"), (sbias[:, :, :], "sbias"),
                              (Vc[:, :, :], "vc")):
                act.dma_start(dst, io[name]).then_inc(s_attc, 16)
            act.dma_start(io["k_kept"], io["k_cache"][:, NT:WIN, :]).then_inc(s_out, 16)
            act.dma_start(io["v_kept"], io["v_cache"][:, NT:WIN, :]).then_inc(s_out, 16)

            act.wait_ge(tile_read.sem, tile_read["K", 1])
            act.dma_start(io["k_new"], KT[:, :, NP_TOK - WIN:N]).then_inc(s_out, 16)
            act.dma_start(io["v_new"][0:P, :], V[:, NQB - 1, :]).then_inc(s_out, 16)
            act.dma_start(io["v_new"][P:P + NS_TOK, :], V[0:NS_TOK, NQB, :]).then_inc(s_out, 16)

            def exps(s):
                par = s % 2
                act.wait_ge(sm_done, s + 1)
                if s < 32:
                    c0 = 0 if s % NQB else P
                    for hd in range(2):
                        ins = fn(SC[:, par, hd, c0:257], SC[:, par, hd, c0:257], ACT.Exp, bias=nm[:, par, hd:hd + 1],
                                 accum_out=dn[:, par, hd:hd + 1])
                else:
                    ins = fn(SC[:, par, 0, 0:CTX + 1], SC[:, par, 0, 0:CTX + 1], ACT.Exp, bias=nm[:, par, 0:1],
                             accum_out=dn[:, par, 0:1])
                ins.then_inc(ex_done, 1)

            def turned(s):
                par = s % 2
                act.wait_ge(pt_done, s + 1)
                if s >= 2:
                    act.wait_ge(pv_done, s - 1)
                if s < 32 and s % NQB:
                    ins = fn(PTs[:, par, :, :], ps[:, 7, :].rearrange("p (u k) -> p u k", k=P), ACT.Copy)
                elif s < 32:
                    ins = fn(PTs[:, par, 1::2, :], ps[:, 7, :].rearrange("p (u k) -> p u k", k=P)[:, 1::2, :], ACT.Copy)
                else:
                    fn(PTs[:, par, 0, :], ps[:, 7, 0:P], ACT.Copy)
                    ins = fn(PTs[0:NS_TOK, par, 1, :], ps[0:NS_TOK, 7, P:2 * P], ACT.Copy)
                ins.then_inc(pt_read, 1)

            for s in range(43):
                if s < 40:
                    exps(s)
                if 1 <= s < 41:
                    turned(s - 1)
                if s >= 5 and (s - 5) % NQB == 0 and (s - 5) // NQB < 8:
                    n = (s - 5) // NQB
                    act.wait_ge(pv_done, NQB * (n + 1))
                    fn(hhi[:, n, 0:NP_TOK], ps[:, 2, :], ACT.Copy).then_inc(o_hi, 1)
                if s >= 35:
                    act.wait_ge(ot_done, s - 34)
                    for t in range(2):
                        e, pb = (s - 3) % 2, (s - 35) // 2
                        q = slice(HD * e, HD * e + HD)
                        src = ps[q, e, t * P:(t + 1) * P].rearrange("p (b g j k) -> p g b j k", b=2, g=2, j=GRP)[:, t]
                        tok = slice(NP_TOK + 2 * NT * pb, NP_TOK + 2 * NT * (pb + 1))
                        ins = fn(hhi[q, GRP * t:GRP * (t + 1), tok].rearrange("p j (b k) -> p b j k", b=2), src,
                                 ACT.Copy)
                    ins.then_inc(o_hi, 1)

            for m in range(KC):
                prepare(1, m, m == 0)

            def ffn(l):
                k = 2 * l + 1
                rms(k, 4, False)

                def hidden(f, first):
                    act.wait_ge(g_read[l], f + 1)
                    if not first:
                        act.wait_ge(u_read[l], f)
                    fn(sg[:, :], gs[:, :], ACT.Silu).then_inc(silu_done[l], 1)
                    act.wait_ge(u_read[l], f + 1)
                    fn(chunk(hhi, f), h32[:, :] if isinstance(f, int) else h32[:, :].unsqueeze(1),
                       ACT.Copy).then_inc(h_hi[l], 1)

                n0 = B_F1[l] + 2

                def split(j, r=0):
                    n = n0 + j
                    act.wait_ge(arrived[n % STAGE], (r + (n // STAGE + 1)) * 16)
                    act.wait_ge(w_used, r * STAGE + (n - (RING - 1)))
                    fn(whi[:, n % RING, :], wst[:, n % STAGE, :], ACT.Copy).then_inc(act_split, 1)

                for f in range(2):
                    split(2 * f)
                    hidden(f, f == 0)
                    split(2 * f + 1)
                with act.Fori(1, FC // 2) as r:
                    for f in range(2):
                        split(2 * f, r)
                        hidden(r * 2 + f, False)
                        split(2 * f + 1, r)
                for m in range(KC):
                    for j in range(3 if m < KC - 1 else 1):
                        split(2 * FC + 3 * m + j)
                    prepare(k + 1, m, m == 0)

            act.wait_ge(s_out, 16 * 5)
            ffn(0)

            act.wait_ge(x_new, 2 * KC)
            for dst, name in ((q1[:, 0:NQB * P], "cm"), (k1[0:NS_TOK, 0:NS_TOK], "cms"), (q2[:, :], "scanm"),
                              (eye8[:, :, :], "eye8")):
                act.dma_start(dst, io[name]).then_inc(s_glac, 16)
            act.dma_start(S0[:, :, :], io["s0"][0]).then_inc(s_s0in, 16)
            rms(2, 0, True)

            def log_term(h):
                act.wait_ge(gv.sem, gv["z", h])
                fn(t2[:, :], t1[:, :], ACT.Abs).then_inc(ga.sem, ga.one("abs", h))
                act.wait_ge(ga.sem, ga["abs", h])
                fn(t2[:, :], t2[:, :], ACT.Exp, scale=-1.0).then_inc(ga.sem, ga.one("exp", h))
                act.wait_ge(ga.sem, ga["exp", h])
                fn(t2[:, :], t2[:, :], ACT.Ln, bias=1.0).then_inc(ga.sem, ga.one("ln", h))

            def decays(h):
                b, g = bb[:, h % 2, :], 1.0 / 16.0
                if h:
                    act.wait_ge(gp.sem, gp["kes", h - 1])
                act.wait_ge(gv.sem, gv["d1", h])
                fn(q1[:, :], t1[:, :], ACT.Exp, scale=g).then_inc(ga.sem, ga.one("e1", h))
                fn(k1[:, :], t1[:, :], ACT.Exp, scale=-g).then_inc(ga.sem, ga.one("e2", h))
                act.wait_ge(gv.sem, gv["d2", h])
                fn(k2[:, :], t2[:, :], ACT.Exp, scale=g).then_inc(ga.sem, ga.one("ek", h))
                fn(dcol[:, h % 2, 0:8], b[:, CH - 1:NP_TOK:CH], ACT.Exp, scale=g)
                fn(dcol[:, h % 2, 8:16], b[:, NP_TOK + NT - 1:N:NT], ACT.Exp, scale=g
                   ).then_inc(ga.sem, ga.one("dec", h))

            def decay_in(h):
                if h:
                    act.wait_ge(gp.sem, gp["o1", h - 1])
                    act.wait_ge(gv.sem, gv["qm", h - 1])
                fn(q2[:, :], bb[:, h % 2, :], ACT.Exp, scale=1.0 / 16.0).then_inc(ga.sem, ga.one("e3", h))

            log_term(0)
            decays(0)
            decay_in(0)
            def output_hi(h):
                act.wait_ge(gv.sem, gv["yt", h])
                for d, y in enumerate((t1, t2)):
                    ins = fn(hhi[:, 2 * h + d, :], y[:, :], ACT.Copy)
                ins.then_inc(ga.sem, ga.one("hi", h))

            def turned_keys(h):
                if h:
                    act.wait_ge(gp.sem, gp["v3", h - 1])
                act.wait_ge(gp.sem, gp["ke", h])
                fn(ke[:, 0:NQB, :], ps[:, 4, :].rearrange("p (t k) -> p t k", k=P), ACT.Copy)
                act.wait_ge(gp.sem, gp["kes", h])
                fn(ke[0:NS_TOK, NQB, :], ps[0:NS_TOK, 5, 0:P], ACT.Copy).then_inc(ga.sem, ga.one("ke", h))

            def outputs(h):
                for o in range(2):
                    act.wait_ge(gp.sem, gp[f"o{o}", h])
                    fn(og[:, 2 * o:2 * o + 2, :], ps[:, 6 + o, :].rearrange("p (t k) -> p t k", k=DV), ACT.Copy)
                act.wait_ge(gp.sem, gp["os", h])
                fn(og[0:NS_TOK, NQB, :], ps[0:NS_TOK, 4, 0:DV], ACT.Copy).then_inc(ga.sem, ga.one("og", h))
                act.wait_ge(ga.sem, ga["og", h])
                for t in range(TT):
                    m = P if t < NQB else NS_TOK
                    ins = fn(junk[0:m, 0:DV], og[0:m, t, :], ACT.Square, accum_out=ss[0:m, 0, t:t + 1])
                    if t < TT - 1:
                        chain.link(ins)
                ins.then_inc(ga.sem, ga.one("sq", h))
                act.wait_ge(ga.sem, ga["sq", h])
                fn(ss[:, 1, 0:NQB], ss[:, 0, 0:NQB], ACT.Sqrt, scale=1.0 / DV, bias=epsc[:, :])
                fn(ss[0:NS_TOK, 1, NQB:TT], ss[0:NS_TOK, 0, NQB:TT], ACT.Sqrt, scale=1.0 / DV,
                   bias=epsc[0:NS_TOK, :]).then_inc(ga.sem, ga.one("rt", h))

            for h in range(GH):
                ahead = head_blocks(h)
                nxt = h + 1 < GH
                for j in range(4):
                    if j < len(ahead) and ahead[j][0] == "r":
                        act.wait_ge(tile_read.sem, tile_read[ahead[j]])
                        fn(silr[:, ahead[j][1], :], rz[:, :], ACT.Silu).then_inc(silr_done, 1)
                    if j == 0:
                        if h:
                            act.wait_ge(gv.sem, gv["v", h - 1])
                            act.dma_start(io["s_sample"][h - 1], S0[:, :, :]).then_inc(s_s0out, 16)
                            output_hi(h - 1)
                        if nxt:
                            log_term(h + 1)
                    if j == 1:
                        if h:
                            act.wait_ge(s_s0out, 16 * h)
                            act.dma_start(S0[:, :, :], io["s0"][h]).then_inc(s_s0in, 16)
                        turned_keys(h)
                    if j == 2:
                        if nxt:
                            decays(h + 1)
                        act.wait_ge(gv.sem, gv["sb", h])
                        act.dma_start(io["s_prompt"][h], S[:, NCH - 1, :]).then_inc(s_sp, 16)
                    if j == 3:
                        outputs(h)
                        if nxt:
                            decay_in(h + 1)
            output_hi(GH - 1)
            act.wait_ge(gv.sem, gv["v", GH - 1])
            act.dma_start(io["s_sample"][GH - 1], S0[:, :, :]).then_inc(s_s0out, 16)

            for m in range(KC):
                prepare(3, m, m == 0)
            act.wait_ge(s_s0out, 16 * GH)
            act.wait_ge(s_sp, 16 * GH)
            ffn(1)
            rms(4, 4, False)


def tables():
    f = np.float32
    t = {}
    t["epsc"] = np.full((P, 1), EPS, f)
    t["mean1"] = np.full((P, P), 1.0 / D, f)
    t["ident"] = np.eye(P, dtype=f)
    dist = np.arange(P)[:, None] + WIN - np.arange(2 * WIN)[None]
    ok = (dist >= 0) & (dist <= WIN)
    heads = [8 * (n // 4) + 4 * hd + n % 4 for n in range(8) for hd in range(2)]
    t["bias"] = np.stack([np.where(ok, -SLOPES[h] * dist.astype(f), f(NEG)).astype(f) for h in heads], 1)
    rows = np.arange(P)
    gg, j, tok = rows // 32 % 2, rows // 8 % 4, rows % 8
    dist = tok[:, None] + WIN - np.arange(CTX)[None]
    ok = (dist >= 0) & (dist <= WIN)
    t["sbias"] = np.stack([np.where(ok, -SLOPES[4 * (2 * gg + e) + j][:, None] * dist.astype(f), f(NEG)).astype(f)
                           for e in range(2)], 1)
    t["bm"] = np.stack([(2 * pb + rows // 64)[:, None] == np.arange(NB)[None] for pb in range(4)], 1).astype(f)
    t["km1"] = (np.arange(NS_TOK)[:, None] // NT == np.arange(NB)[None]).astype(f)
    s, q = np.arange(P)[:, None], np.arange(P)[None]
    t["cm"] = np.tile(((s // CH == q // CH) & (s <= q)).astype(f), (1, 4))
    s, q = np.arange(NS_TOK)[:, None], np.arange(NS_TOK)[None]
    t["cms"] = ((s // NT == q // NT) & (s <= q)).astype(f)
    t["eye8"] = np.broadcast_to(np.eye(NB, dtype=f), (P, NB, NB)).copy()
    n = np.arange(N)
    starts = np.where(n < NP_TOK, n % CH == 0, (n - NP_TOK) % NT == 0)
    t["scanm"] = np.broadcast_to(f(1.0) - starts.astype(f), (P, N))
    return t


def tiles_of(w):
    k = w.shape[1] // P
    return w.reshape(w.shape[0] // P, P, k, P).transpose(2, 1, 0, 3)


def weight_blocks(w_attn_in, w_attn_out, w_gla_in, w_gla_out, w_ffn_in, w_ffn_out):
    out = []

    def add(a):
        a = np.ascontiguousarray(a).reshape(a.shape[0], P, -1)
        if a.shape[2] < 1024:
            a = np.concatenate([a, np.zeros((a.shape[0], P, 1024 - a.shape[2]), a.dtype)], 2)
        out.append(a)

    def moving(w, per):
        add(w.reshape(KC // per, per, P, w.shape[1]).transpose(0, 2, 1, 3))

    def ffn(l):
        g, u = tiles_of(w_ffn_in[l][:, :FF]), tiles_of(w_ffn_in[l][:, FF:])
        add(np.stack([g, u], 1).reshape(2 * FC, P, KC * P))
        d = np.concatenate([w_ffn_out[l], np.zeros((2 * P, D), w_ffn_out.dtype)], 0)
        add(d.reshape(3, KC, P, KC, P).transpose(3, 0, 2, 1, 4).reshape(3 * KC, P, KC * P))

    wi, wo = w_attn_in[0], w_attn_out[0]
    moving(wi[:, 1280:1536], 4)
    add(tiles_of(wi[:, 1024:1280]))
    add(tiles_of(wi[:, :1024].reshape(D, 2, 2, 4, HD).transpose(0, 1, 3, 2, 4).reshape(D, D)))
    add(tiles_of(wo.reshape(2, 2, 4, HD, D).transpose(0, 2, 1, 3, 4).reshape(D, D)))
    ffn(0)
    wg = w_gla_in[0]
    q, k, v, r, gt = np.split(wg, [512, 1024, 2048, 3072], axis=1)
    moving(v[:, :512], 2)
    add(tiles_of(np.concatenate([gt, np.zeros((D, P - RANK), gt.dtype)], 1)))
    moving(v[:, 512:], 2)
    parts = {"q": tiles_of(q), "k": tiles_of(k), "r": tiles_of(r)}
    for kind, i in [("q", 0), ("k", 0)] + [b for h in range(GH) for b in head_blocks(h)]:
        add(parts[kind][i:i + 1])
    add(tiles_of(w_gla_out[0]))
    ffn(1)
    return np.concatenate(out, 0)


def by_feature(a):
    a = np.moveaxis(a, -1, 0)
    return np.moveaxis(a.reshape((KC, P) + a.shape[1:]), 0, 1)


def kernel(x_prompt, x_sample, cache_k, cache_v, state_gla, norm_mix, norm_ffn, norm_final,
           w_attn_in, w_attn_out, attn_sinks, w_gla_in, w_gla_gate_up, b_gla_gate, gla_out_norm,
           w_gla_out, w_ffn_in, w_ffn_out):
    import concourse.bacc as bacc
    from concourse.bass_utils import run_bass_kernel_spmd

    args = [np.asarray(a) for a in (w_attn_in, w_attn_out, w_gla_in, w_gla_out, w_ffn_in, w_ffn_out)]
    x_prompt, x_sample, cache_k, cache_v, state_gla = (np.asarray(a) for a in
                                                       (x_prompt, x_sample, cache_k, cache_v, state_gla))
    feed = dict(tables())
    feed["w_blocks"] = weight_blocks(*args)
    feed["x"] = by_feature(np.concatenate([x_prompt[0], x_sample.reshape(NS_TOK, D)], 0))
    nx, nf = np.asarray(norm_mix), np.asarray(norm_ffn)
    feed["gains"] = by_feature(np.stack([nx[0], nf[0], nx[1], nf[1], np.asarray(norm_final)], 0)).transpose(0, 2, 1)
    sinks = np.asarray(attn_sinks)[0]
    feed["sinkp"] = np.broadcast_to(sinks.reshape(2, 2, 4).transpose(0, 2, 1).reshape(8, 2), (P, 8, 2))
    rows = np.arange(P)
    feed["sinks"] = np.stack([sinks[4 * (2 * (rows // 32 % 2) + e) + rows // 8 % 4] for e in range(2)], 1)
    feed["bgate"] = np.asarray(b_gla_gate)[0].reshape(GH, P).T
    feed["gnorm"] = np.asarray(gla_out_norm)[0].reshape(2, P).T
    feed["wup"] = np.asarray(w_gla_gate_up)[0].reshape(RANK, GH, P)
    feed["k_cache"] = cache_k[0].reshape(NB, WIN, 256)
    feed["v_cache"] = cache_v[0].reshape(NB, WIN, 256)
    feed["ktx"] = cache_k[0].reshape(NB, WIN, 2, P).transpose(3, 2, 0, 1)
    feed["vc"] = cache_v[0].reshape(NB, WIN, 256).transpose(1, 0, 2)
    feed["s0"] = state_gla[0].transpose(1, 2, 0, 3)
    feed = {k: np.ascontiguousarray(v) for k, v in feed.items()}

    nc = bacc.Bacc("TRN2", target_bir_lowering=False, num_devices=1)
    io = {k: nc.dram_tensor(k + "_in", v.shape, mybir.dt.from_np(v.dtype), kind="ExternalInput").ap()
          for k, v in feed.items()}
    outs = {"y": (P, KC, N), "k_new": (P, 2, WIN + NS_TOK), "v_new": (WIN + NS_TOK, 256),
            "k_kept": (NB, WIN - NT, 256), "v_kept": (NB, WIN - NT, 256),
            "s_prompt": (GH, DK, DV), "s_sample": (GH, DK, NB, DV)}
    for k, shape in outs.items():
        io[k] = nc.dram_tensor(k + "_out", shape, F32, kind="ExternalOutput").ap()
    build(nc, io)
    got = run_bass_kernel_spmd(nc, [{k + "_in": v for k, v in feed.items()}], core_ids=[0]).results[0]
    got = {k: got[k + "_out"] for k in outs}

    y = got["y"].transpose(2, 1, 0).reshape(N, D)
    k_new = got["k_new"].transpose(2, 1, 0).reshape(WIN + NS_TOK, 256)
    heads = lambda a: np.ascontiguousarray(a).reshape(a.shape[:-1] + (NKV, HD))[None]

    def window(kept, new):
        return heads(np.concatenate([kept, new[WIN:].reshape(NB, NT, 256)], 1))

    return (np.ascontiguousarray(y[:NP_TOK])[None], np.ascontiguousarray(y[NP_TOK:]).reshape(NB, NT, D),
            heads(k_new[:WIN][None]), heads(got["v_new"][:WIN][None]),
            np.ascontiguousarray(got["s_prompt"])[None, None],
            window(got["k_kept"], k_new), window(got["v_kept"], got["v_new"]),
            np.ascontiguousarray(got["s_sample"].transpose(2, 0, 1, 3))[None])
```
